# Optimizing a Trainium2 kernel written in Bass

```python
import jax, jax.numpy as jnp
from jax import lax
import numpy as np

D_MODEL = 2048
BATCH = 1
SEQ = 512
DEPTH = 1
DEC_BATCH = 8
DEC_SEQ = 8
PAST_LEN = 512
PAGE_SIZE = 128

HEAD_DIM = 128
ATTN_HEADS = 8
DIL_GROUPS = ((128, 1), (512, 4), (2048, 16))
N_DIL = len(DIL_GROUPS)
ATTN_WIDTH = ATTN_HEADS * HEAD_DIM
QKV_WIDTH = N_DIL * ATTN_WIDTH
CHUNK = 128
GMLP_GROUPS = 8
GMLP_GROUP_DIM = 128
GMLP_WIDTH = GMLP_GROUPS * GMLP_GROUP_DIM
ROPE_THETA = 10000.0
LN_EPS = 1e-5
DN_ALPHA = float(2 * DEPTH) ** 0.25
DN_BETA = float(8 * DEPTH) ** -0.25
SPLIT_SIZES = (QKV_WIDTH, QKV_WIDTH, QKV_WIDTH, ATTN_WIDTH, GMLP_WIDTH, GMLP_WIDTH, GMLP_WIDTH, D_MODEL, D_MODEL)
SPLIT_POINTS = tuple(int(s) for s in np.cumsum(SPLIT_SIZES)[:-1])
IN_WIDTH = int(sum(SPLIT_SIZES))

kernel_name = "gated_dilated_attn_gmlp_deepnorm_step"

def layer_norm(x, g, b):
    xf = x.astype(jnp.float32)
    mu = jnp.mean(xf, axis=-1, keepdims=True)
    var = jnp.mean(jnp.square(xf - mu), axis=-1, keepdims=True)
    return ((xf - mu) * lax.rsqrt(var + LN_EPS) * g.astype(jnp.float32) + b.astype(jnp.float32)).astype(x.dtype)

def rope(x, pos):
    half = x.shape[-1] // 2
    inv = ROPE_THETA ** (-jnp.arange(0, half, dtype=jnp.float32) * 2.0 / x.shape[-1])
    ang = pos.astype(jnp.float32)[:, None] * inv[None, :]
    bshape = (pos.shape[0],) + (1,) * (x.ndim - 3) + (half,)
    cos = jnp.cos(ang).reshape(bshape)
    sin = jnp.sin(ang).reshape(bshape)
    xf = x.astype(jnp.float32)
    x1, x2 = xf[..., :half], xf[..., half:]
    return jnp.concatenate([x1 * cos - x2 * sin, x2 * cos + x1 * sin], axis=-1).astype(x.dtype)

def project_in(x, w_in, b_in):
    h = x @ w_in + b_in
    q, k, v, z_b, u, v_a, z_a, g_a, g_b = jnp.split(h, SPLIT_POINTS, axis=-1)
    shp = x.shape[:-1] + (N_DIL, ATTN_HEADS, HEAD_DIM)
    return q.reshape(shp), k.reshape(shp), v.reshape(shp), z_b, u, v_a, z_a, g_a, g_b

def dilated_attn_prompt(q, k, v, window, dil):
    B, S, H, dh = q.shape
    band = window // dil
    L = S // dil
    nb = -(-L // band)
    Lp = nb * band

    def sub(x):
        return jnp.pad(x.reshape(B, L, dil, H, dh), ((0, 0), (0, Lp - L), (0, 0), (0, 0), (0, 0)))

    def win(x):
        x = jnp.pad(x, ((0, 0), (band, 0), (0, 0), (0, 0), (0, 0))).reshape(B, nb + 1, band, dil, H, dh)
        return jnp.concatenate([x[:, :-1], x[:, 1:]], axis=2)

    qb = sub(q).reshape(B, nb, band, dil, H, dh).astype(jnp.float32)
    kw = win(sub(k)).astype(jnp.float32)
    vw = win(sub(v)).astype(jnp.float32)
    s = jnp.einsum('bnqrhe,bnkrhe->bnrhqk', qb, kw) * (dh ** -0.5)
    qi = jnp.arange(nb)[:, None, None] * band + jnp.arange(band)[None, :, None]
    ki = jnp.arange(nb)[:, None, None] * band - band + jnp.arange(2 * band)[None, None, :]
    mask = (ki >= 0) & (qi - ki >= 0) & (qi - ki <= band)
    s = jnp.where(mask[None, :, None, None], s, -jnp.inf)
    m = jnp.max(s, axis=-1, keepdims=True)
    p = jnp.exp(s - m)
    den = jnp.sum(p, axis=-1)
    lse = m[..., 0] + jnp.log(den)
    o = jnp.einsum('bnrhqk,bnkrhe->bnqrhe', p, vw) / jnp.transpose(den, (0, 1, 4, 2, 3))[..., None]
    o = o.reshape(B, Lp, dil, H, dh)[:, :L].reshape(B, S, H, dh)
    lse = jnp.transpose(lse, (0, 1, 4, 2, 3)).reshape(B, Lp, dil, H)[:, :L].reshape(B, S, H)
    return o, lse

def dilated_attn_sample(q, k_new, v_new, k_cache, v_cache, window, dil):
    T, dh = q.shape[1], q.shape[-1]
    band = window // dil
    Wc = k_cache.shape[1]
    k_all = jnp.concatenate([k_cache, k_new], axis=1)
    v_all = jnp.concatenate([v_cache, v_new], axis=1)
    idx = Wc + jnp.arange(T)[:, None] - dil * jnp.arange(band + 1)[None, :]
    valid = idx >= 0
    idx = jnp.maximum(idx, 0)
    kg = k_all[:, idx].astype(jnp.float32)
    vg = v_all[:, idx].astype(jnp.float32)
    s = jnp.einsum('bthe,btjhe->bthj', q.astype(jnp.float32), kg) * (dh ** -0.5)
    s = jnp.where(valid[None, :, None, :], s, -jnp.inf)
    m = jnp.max(s, axis=-1, keepdims=True)
    p = jnp.exp(s - m)
    den = jnp.sum(p, axis=-1)
    o = jnp.einsum('bthj,btjhe->bthe', p, vg) / den[..., None]
    return o, m[..., 0] + jnp.log(den)

def merge_dilation_groups(outs):
    o = jnp.stack([o_g for o_g, _ in outs])
    lse = jnp.stack([l_g for _, l_g in outs])
    wts = jax.nn.softmax(lse, axis=0)
    return jnp.einsum('gbsh,gbshe->bshe', wts, o)

def gmlp_branch(u, v, z, ln_g, ln_b, w_s, b_s):
    Bn, S, _ = u.shape
    rows = min(CHUNK, S)
    u = jax.nn.gelu(u, approximate=False)
    v = layer_norm(jax.nn.gelu(v, approximate=False), ln_g, ln_b)
    vr = v.reshape(Bn, S // rows, rows, GMLP_GROUPS, GMLP_GROUP_DIM)
    w_c = jnp.tril(w_s[:, :rows, :rows])
    mixed = jnp.einsum('gij,bcjgd->bcigd', w_c, vr) + jnp.swapaxes(b_s[:, :rows], 0, 1)[:, :, None]
    mixed = mixed.reshape(Bn, S, GMLP_WIDTH)
    return u * mixed * jax.nn.silu(z), v

def mix_and_norm(x, y_a, o_b, z_b, g_a, g_b, w_o_a, w_o_b, w_out, ln_g, ln_b):
    y_b = o_b.reshape(o_b.shape[:2] + (ATTN_WIDTH,)).astype(x.dtype) * jax.nn.silu(z_b)
    merged = jax.nn.sigmoid(g_a) * (y_a @ w_o_a) + jax.nn.sigmoid(g_b) * (y_b @ w_o_b)
    return layer_norm(DN_ALPHA * x + merged @ w_out, ln_g, ln_b)

def setup_inputs(seed: int = 0) -> dict:
    key = jax.random.key(seed)
    ks = jax.random.split(key, 24)
    f32 = jnp.float32

    def nrm(k, shape, scale):
        return jax.random.normal(k, shape, f32) * scale

    inp = {}
    inp['x_prompt'] = nrm(ks[0], (BATCH, SEQ, D_MODEL), 1.0)
    inp['x_sample'] = nrm(ks[1], (DEC_BATCH, DEC_SEQ, D_MODEL), 1.0)
    for g, (win, _) in enumerate(DIL_GROUPS):
        keep = min(win, PAST_LEN)
        shp = (DEPTH, DEC_BATCH, keep, ATTN_HEADS, HEAD_DIM)
        inp['cache_k_w%d' % win] = nrm(ks[2 + 2 * g], shp, 1.0)
        inp['cache_v_w%d' % win] = nrm(ks[3 + 2 * g], shp, 1.0)
    inp['w_in'] = nrm(ks[8], (DEPTH, D_MODEL, IN_WIDTH), D_MODEL ** -0.5)
    inp['b_in'] = nrm(ks[9], (DEPTH, IN_WIDTH), 0.01)
    inp['w_s'] = nrm(ks[10], (DEPTH, GMLP_GROUPS, CHUNK, CHUNK), CHUNK ** -0.5)
    inp['b_s'] = 1.0 + nrm(ks[11], (DEPTH, GMLP_GROUPS, CHUNK), 0.1)
    inp['ln_v_g'] = 1.0 + nrm(ks[12], (DEPTH, GMLP_WIDTH), 0.05)
    inp['ln_v_b'] = nrm(ks[13], (DEPTH, GMLP_WIDTH), 0.02)
    inp['w_o_a'] = nrm(ks[14], (DEPTH, GMLP_WIDTH, D_MODEL), DN_BETA * GMLP_WIDTH ** -0.5)
    inp['w_o_b'] = nrm(ks[15], (DEPTH, ATTN_WIDTH, D_MODEL), DN_BETA * ATTN_WIDTH ** -0.5)
    inp['w_out'] = nrm(ks[16], (DEPTH, D_MODEL, D_MODEL), DN_BETA * D_MODEL ** -0.5)
    inp['ln_g'] = 1.0 + nrm(ks[17], (DEPTH, D_MODEL), 0.05)
    inp['ln_b'] = nrm(ks[18], (DEPTH, D_MODEL), 0.02)
    return inp

def reference(x_prompt, x_sample, cache_k_w128, cache_v_w128, cache_k_w512, cache_v_w512,
              cache_k_w2048, cache_v_w2048, w_in, b_in, w_s, b_s, ln_v_g, ln_v_b,
              w_o_a, w_o_b, w_out, ln_g, ln_b):
    S = x_prompt.shape[1]
    T = x_sample.shape[1]
    pos_p = jnp.arange(S, dtype=jnp.int32)
    pos_s = PAST_LEN + jnp.arange(T, dtype=jnp.int32)
    caches_k = (cache_k_w128, cache_k_w512, cache_k_w2048)
    caches_v = (cache_v_w128, cache_v_w512, cache_v_w2048)
    new_pk = [[] for _ in DIL_GROUPS]
    new_pv = [[] for _ in DIL_GROUPS]
    new_sk = [[] for _ in DIL_GROUPS]
    new_sv = [[] for _ in DIL_GROUPS]
    new_gv = []
    xp, xs = x_prompt, x_sample
    for l in range(DEPTH):
        q, k, v, z_b, u, v_a, z_a, g_a, g_b = project_in(xp, w_in[l], b_in[l])
        q = rope(q, pos_p)
        k = rope(k, pos_p)
        outs = []
        for g, (win, dil) in enumerate(DIL_GROUPS):
            outs.append(dilated_attn_prompt(q[:, :, g], k[:, :, g], v[:, :, g], win, dil))
            keep = min(win, S)
            new_pk[g].append(k[:, S - keep:, g])
            new_pv[g].append(v[:, S - keep:, g])
        o_b = merge_dilation_groups(outs)
        y_a, _ = gmlp_branch(u, v_a, z_a, ln_v_g[l], ln_v_b[l], w_s[l], b_s[l])
        xp = mix_and_norm(xp, y_a, o_b, z_b, g_a, g_b, w_o_a[l], w_o_b[l], w_out[l], ln_g[l], ln_b[l])

        q, k, v, z_b, u, v_a, z_a, g_a, g_b = project_in(xs, w_in[l], b_in[l])
        q = rope(q, pos_s)
        k = rope(k, pos_s)
        outs = []
        for g, (win, dil) in enumerate(DIL_GROUPS):
            outs.append(dilated_attn_sample(q[:, :, g], k[:, :, g], v[:, :, g],
                                            caches_k[g][l], caches_v[g][l], win, dil))
            new_sk[g].append(k[:, :, g])
            new_sv[g].append(v[:, :, g])
        o_b = merge_dilation_groups(outs)
        y_a, v_rows = gmlp_branch(u, v_a, z_a, ln_v_g[l], ln_v_b[l], w_s[l], b_s[l])
        new_gv.append(v_rows)
        xs = mix_and_norm(xs, y_a, o_b, z_b, g_a, g_b, w_o_a[l], w_o_b[l], w_out[l], ln_g[l], ln_b[l])

    new_k_w128_prompt = jnp.stack(new_pk[0])
    new_v_w128_prompt = jnp.stack(new_pv[0])
    new_k_w512_prompt = jnp.stack(new_pk[1])
    new_v_w512_prompt = jnp.stack(new_pv[1])
    new_k_w2048_prompt = jnp.stack(new_pk[2])
    new_v_w2048_prompt = jnp.stack(new_pv[2])
    new_k_w128_sample = jnp.stack(new_sk[0])
    new_v_w128_sample = jnp.stack(new_sv[0])
    new_k_w512_sample = jnp.stack(new_sk[1])
    new_v_w512_sample = jnp.stack(new_sv[1])
    new_k_w2048_sample = jnp.stack(new_sk[2])
    new_v_w2048_sample = jnp.stack(new_sv[2])
    new_gmlp_v_sample = jnp.stack(new_gv)
    return (xp, xs,
            new_k_w128_prompt, new_v_w128_prompt, new_k_w512_prompt, new_v_w512_prompt,
            new_k_w2048_prompt, new_v_w2048_prompt,
            new_k_w128_sample, new_v_w128_sample, new_k_w512_sample, new_v_w512_sample,
            new_k_w2048_sample, new_v_w2048_sample,
            new_gmlp_v_sample)


_drawn_inputs = setup_inputs


def setup_inputs(seed=0):
    import zlib

    import numpy as np

    out = dict(_drawn_inputs(seed))
    spreads = {}
    factors = {'cache_k_w128': 8.0,
     'cache_v_w128': 8.0,
     'cache_k_w512': 8.0,
     'cache_v_w512': 8.0,
     'cache_k_w2048': 8.0,
     'cache_v_w2048': 8.0,
     'b_in': 4.732,
     'b_s': 8.0,
     'ln_v_b': 2.754,
     'w_o_b': 3.869,
     'ln_b': 2.846}
    for name, (base, spread) in spreads.items():
        noise = np.random.default_rng([zlib.crc32(name.encode()), seed]).standard_normal(out[name].shape)
        drawn = base * np.exp(spread * noise) if base else spread * noise
        out[name] = __import__('jax').numpy.asarray(drawn.astype(out[name].dtype))
    for name, factor in factors.items():
        out[name] = (out[name] * factor).astype(out[name].dtype)
    return out
```

```python
from contextlib import ExitStack

import numpy as np

import concourse.bass as bass
from concourse import mybir

F32 = mybir.dt.float32
F32R = mybir.dt.float32r
ALU = mybir.AluOpType
ACT = mybir.ActivationFunctionType

P = 128
D = 2048
SEQ = 512
DEC_B = 8
DEC_T = 8
SAMP = DEC_B * DEC_T
TOK = SEQ + SAMP
HALF = TOK // 2
HEADS = 8
GROUPS = 3
KB = D // P
QB = 4
WIDTH = HEADS * P
IN_WIDTH = 136 * P
COL_K, COL_V = GROUPS * WIDTH, 2 * GROUPS * WIDTH
COL_ZB = 3 * GROUPS * WIDTH
COL_U, COL_VA, COL_ZA = COL_ZB + WIDTH, COL_ZB + 2 * WIDTH, COL_ZB + 3 * WIDTH
COL_GA = COL_ZB + 4 * WIDTH
COL_GB = COL_GA + D
PAST = 512
LN_EPS = 1e-5
ALPHA = float(2.0) ** 0.25
SCALE = float(P) ** -0.5
MASKED = -3.0e38
CACHED = 7 * P
NEW = GROUPS * SAMP

CHUNKS = 10
SLOTS = 4 * CHUNKS
LEAD = 3

Q_GATE = 9 * SLOTS
Q_A = Q_GATE + 7 * 8
Q_B = Q_A + 16 * 6
Q_OUT = Q_B + 16 * 6
Q_END = Q_OUT + 16 * 4
R_GATE = 9 * CHUNKS
R_A = R_GATE + 14
R_B = R_A + 16
R_OUT = R_B + 16


def tile_rows(c):
    return P if c < 4 else SAMP


def half_cols(h):
    return slice(h * (D // 2), (h + 1) * (D // 2))


def slot_qk(i):
    return 18 + 3 * i


def slot_turn_p(i):
    return 20 + 3 * i


def slot_pv(i):
    return 22 + 3 * i


SLOT_K, SLOT_V = [11, 24, 35], [13, 25, 37]
SLOT_VS = [30, 32, 33, 34, 35, 36, 37, 38]
SLOT_PVS = [32, 32, 33, 34, 35, 36, 37, 38]


def turn_names(attends, kind):
    out = []
    for s in range(SLOTS):
        if attends:
            if s % 2 == 0 and s < 16:
                out += [(s, ("kt", s // 2, 0)), (s, ("kt", s // 2, 1))]
            for i in range(4):
                if s == slot_turn_p(i):
                    out += [(s, ("pt", i, 0)), (s, ("pt", i, 1))]
            if s == slot_pv(3):
                out += [(s, ("pts", 0)), (s, ("pts", 1))]
        if kind == "head":
            for g in range(GROUPS):
                if s == SLOT_K[g]:
                    out += [(s, ("k", g, 0)), (s, ("k", g, 1))]
                if s == SLOT_V[g]:
                    out += [(s, ("v", g, 0)), (s, ("v", g, 1))]
        else:
            for j in range(8):
                if s == 4 * j + 5:
                    out += [(s, ("va", j, 0)), (s, ("va", j, 1))]
    return out


def kt_before(names, n):
    return sum(x[0] == "kt" for x in names[:n]) if n and names[n - 1][0] == "kt" else 0


TURNS_FIRST = turn_names(False, "head")
TURNS_HEAD = turn_names(True, "head")
TURNS_GMLP = turn_names(True, "gmlp")


def turns_of(f):
    if isinstance(f, int) and f == 0:
        return TURNS_FIRST, 0
    before = len(TURNS_FIRST) + len(TURNS_HEAD) * (f - 1)
    return (TURNS_GMLP if isinstance(f, int) and f == 8 else TURNS_HEAD), before


TURNS_ALL = len(TURNS_FIRST) + 7 * len(TURNS_HEAD) + len(TURNS_GMLP)

SCORES = (["cache", "new", ("qk", 0), ("qk", 1), ("pv", 0), ("qk", 2), ("pv", 1), ("qk", 3),
           ("pv", 2), ("pv", 3), "cached_pv", "sample_out"])
N_SC = len(SCORES)
S_ATT = HEADS * N_SC
SIGNALLED = [n for n in SCORES if n not in ("cache", "cached_pv")]
N_SIG = len(SIGNALLED)
S_SIG = HEADS * N_SIG
CHAIN_FIRST, CHAIN_HEAD = 18, 34
GATE_TABLES = 16 * (3 + 4 + DEC_B)


def build(nc, x_prompt, x_sample, ck, cv, w_in, b_in, w_s, b_s, ln_v_g, ln_v_b, w_o_a, w_o_b,
          w_out, ln_g, ln_b, c_cos, c_sin, c_mask, c_smask, c_tri, c_tri8, c_id,
          y_prompt, y_sample, nk_p, nv_p, nk_s, nv_s, n_gv):
    nc.disable_value_cache = True
    yb_d = nc.dram_tensor("yb_scratch", (HEADS, P, TOK), F32, kind="Internal").ap()
    with ExitStack() as ctx:
        sem = lambda name: ctx.enter_context(nc.semaphore(name))
        place = [16512]
        top = 229344

        def sb(name, shape, dt=F32, at=None):
            size = 4 * int(np.prod(shape[1:]))
            if at is None:
                at = place[0]
                place[0] += -(-size // 32) * 32
            assert at + size <= top, (name, at + size)
            return nc.alloc_sbuf_tensor_at(name, list(shape), dt, offset=at)

        xh = sb("xh", [P, KB, TOK], F32R)
        xl = sb("xl", [P, KB, TOK], F32R)
        raw = sb("raw", [P, 4, QB, P])
        wh = sb("wh", [P, 4, QB, P], F32R)
        wl = sb("wl", [P, 4, QB, P], F32R)
        ident = sb("ident", [P, P])
        bias = sb("bias", [P, 136])
        stage = sb("stage", [P, 2, TOK])
        small = sb("small", [P, 32])
        work = place[0]
        qkv = sb("qkv", [P, 2, 2 * GROUPS * TOK + GROUPS * 5 * P])
        knat = sb("knat", [P, 5, P])
        vl = sb("vl", [P, 4, 7, P], F32R, at=place[0])
        cache = sb("cache", [P, 4, 7, P])
        qzh = sb("qzh", [P, GROUPS, TOK], F32R)
        qzl = sb("qzl", [P, GROUPS, TOK], F32R)
        sc = sb("sc", [P, 6 * P], at=place[0])
        vh = [sb("vh0", [P, 7, P], F32R, at=place[0]), sb("vh1", [P, 7, P], F32R, at=place[0] + CACHED * 4)]
        kth = sb("kth", [P, CACHED], F32R)
        pt = sb("pt", [P, 6 * P], at=place[0])
        ktl = sb("ktl", [P, CACHED], F32R)
        psl = sb("psl", [P, 7, SAMP], F32R, at=place[0])
        osm = sb("osm", [DEC_T, 8 * P], at=place[0])
        otmp = sb("otmp", [P, SAMP], at=place[0] + 8 * P * 4)
        ss = sb("ss", [SAMP, CACHED + NEW])
        psh = sb("psh", [P, 7, SAMP], F32R)
        psn = sb("psn", [SAMP, GROUPS, SAMP])
        mask = sb("mask", [P, 9 * P])
        smask = sb("smask", [SAMP, CACHED + NEW])
        cos = sb("cos", [P, TOK])
        sin = sb("sin", [P, TOK])
        rot = sb("rot", [P, TOK])
        zt = sb("zt", [P, TOK])
        yt = sb("yt", [P, TOK])
        vn = sb("vn", [P, 5, WIDTH], at=work)
        place[0] = work + 21504
        tg = sb("tg", [P, 8, TOK])
        wsn = sb("wsn", [P, 8, P])
        wct = sb("wct", [P, 8, P])
        bsb = sb("bsb", [P, 8, P])
        w8 = sb("w8", [SAMP, 8, SAMP])
        w8n = sb("w8n", [SAMP, 8, SAMP])
        lnvg = sb("lnvg", [P, WIDTH])
        lnvb = sb("lnvb", [P, WIDTH])
        tri = sb("tri", [P, P])
        tri8 = sb("tri8", [SAMP, SAMP])
        ym = sb("ym", [P, TOK])
        vstat = sb("vstat", [P, 5, 2, 6])
        vmv = sb("vmv", [P, 5, 2])
        yh = sb("yh", [P, 8, TOK], F32R)
        yl = sb("yl", [P, 8, TOK], F32R)
        wss = sb("wss", [P, 8, P], at=place[0] - 8 * P * 4)
        ybraw = sb("ybraw", [P, 8, TOK], at=work)
        m = sb("m", [P, KB, TOK], at=work + 21504)
        mtmp = sb("mtmp", [P, TOK], at=work + 18432)
        xn0 = sb("xn0", [P, 5, D], at=work)
        bn0 = sb("bn0", [P, P], at=work + 40960)
        bn1 = sb("bn1", [8, P], at=work + 41984)
        res = sb("res", [P, 5, D], at=work + 21504 + KB * TOK * 4)
        place[0] = work + 21504 + KB * TOK * 4 + 40960
        xn = sb("xn", [P, 2, 5, P])
        rstat = sb("rstat", [P, 5, KB, 6])
        rmv = sb("rmv", [P, 5, 2])
        shift = sb("shift", [P, 5])
        lng = sb("lng", [P, D], at=work)
        lnb = sb("lnb", [P, D], at=work + 8192)

        GQ = GROUPS * TOK
        qT = [[qkv[:, p, g * TOK:(g + 1) * TOK] for g in range(GROUPS)] for p in range(2)]
        kT = [[qkv[:, p, GQ + g * TOK:GQ + (g + 1) * TOK] for g in range(GROUPS)] for p in range(2)]
        vN = [[qkv[:, p, 2 * GQ + g * 5 * P:2 * GQ + (g + 1) * 5 * P].rearrange("p (c d) -> p c d", c=5)
               for g in range(GROUPS)] for p in range(2)]

        acc = ctx.enter_context(nc.psum_tensor("acc", [P, 2, 1024], F32))
        turn = ctx.enter_context(nc.psum_tensor("turn", [P, 2, 512], F32))
        scp = ctx.enter_context(nc.psum_tensor("scp", [P, 1024], F32))
        x_bank = lambda k: (scp[:], turn[:].rearrange("p b c -> p (b c)"), acc[:, 1, :])[k % 3]
        accv = [acc[:, p, :].rearrange("p (h c) -> p h c", h=2)[:, :, 0:HALF] for p in range(2)]

        w_loaded = [sem(f"w_loaded{i}") for i in range(4)]
        w_round = sem("w_round")
        w_split = sem("w_split")
        w_used = sem("w_used")
        acc_read = sem("acc_read")
        merged = sem("merged")
        x_loaded = [sem(f"x_loaded{c}") for c in range(4)]
        ident_in, b_loaded, consts = sem("ident_in"), sem("b_loaded"), sem("consts")
        x_turned, x_round, x_split = sem("x_turned"), sem("x_round"), sem("x_split")
        b_turned, b_ready, zeroed = sem("b_turned"), sem("b_ready"), sem("zeroed")
        roped, q_spread = sem("roped"), sem("q_spread")
        turned, turn_read = sem("turned"), sem("turn_read")
        scored, score_read = sem("scored"), sem("score_read")
        kt_split, keys_used = sem("kt_split"), sem("keys_used")
        cache_in = [sem(f"cache_in{i}") for i in range(4)]
        v_round, v_split, ps_split, pv_used = sem("v_round"), sem("v_split"), sem("ps_split"), sem("pv_used")
        biased, expd, normed = sem("biased"), sem("expd"), sem("normed")
        y_done, y_stored = sem("y_done"), sem("y_stored")
        k_stored, v_stored = sem("k_stored"), sem("v_stored")
        vector_done = sem("vector_done")
        gated, g_loaded, g_zero, lnv_in = sem("gated"), sem("g_loaded"), sem("g_zero"), sem("lnv_in")
        v_var, v_sqrt, v_norm, gv_stored = sem("v_var"), sem("v_sqrt"), sem("v_norm"), sem("gv_stored")
        b_product, v_sorted, w_sorted = sem("b_product"), sem("v_sorted"), sem("w_sorted")
        y_mixed = sem("y_mixed")
        y_ready, y_round, y_split = sem("y_ready"), sem("y_round"), sem("y_split")
        yb_loaded, yb_round, yb_split = sem("yb_loaded"), sem("yb_round"), sem("yb_split")
        m_round, m_split = sem("m_round"), sem("m_split")
        out_turned, out_read = sem("out_turned"), sem("out_read")
        xn_in = [sem("xn_in0"), sem("xn_in1")]
        ln_in, o_var, o_sqrt = sem("ln_in"), sem("o_var"), sem("o_sqrt")
        o_norm_v, o_norm_p = sem("o_norm_v"), sem("o_norm_p")
        o_stored = [sem(f"o_stored{c}") for c in range(5)]
        o_gained, o_centred = sem("o_gained"), sem("o_centred")
        o_scaled, o_stats = sem("o_scaled"), sem("o_stats")

        block = ctx.enter_context(nc.Block())
        ds = bass.ds

        def frame_cols(f, j):
            if isinstance(f, int) and f == 8:
                return COL_VA + j * P if j < 8 else (COL_U if j == 8 else COL_ZA)
            if j == 9:
                return COL_ZB + f * P
            return (0, COL_K, COL_V)[j % 3] + (j // 3) * WIDTH + f * P

        def frames(eng, frame):
            frame(0, 0)
            frame(1, 1)
            with eng.Fori(1, 4) as i:
                frame(2 * i, 0)
                frame(2 * i + 1, 1)
            frame(8, 0)

        def score_no(f, name):
            return N_SC * (f - 1) + SCORES.index(name) + 1

        def signal_no(f, name):
            return N_SIG * (f - 1) + SIGNALLED.index(name) + 1

        @block.sync
        def _(sp):
            def load(q, u, src):
                if not (isinstance(q, int) and q < 4):
                    sp.wait_ge(w_split, q - 3)
                sp.dma_start(raw[:, u % 4, :, :], src).then_inc(w_loaded[u % 4], 16)

            def block_of(w, k, col):
                return w[0, k * P:(k + QB) * P, ds(col, P)].rearrange("(k p) n -> p k n", p=P)

            def load_x(c):
                cols = slice(c * QB * P, (c + 1) * QB * P)
                sp.dma_start(xn0[:, 0:4, cols], x_prompt[0].rearrange("(i r) d -> i r d", r=4)[:, :, cols]
                             ).then_inc(x_loaded[c], 16)
                sp.dma_start(xn0[0:SAMP, 4, cols], x_sample.rearrange("b t d -> (b t) d")[:, cols]
                             ).then_inc(x_loaded[c], 16)

            def load_cache(h, src, b):
                slot = b % 2 if src is ck else b % 4
                dst = cache[:, slot, :, :]
                rows = [c[0, b, :, ds(h, 1), :].rearrange("n o d -> n (o d)") for c in src]
                sp.dma_start(dst[:, 0, :], rows[0]).then_inc(cache_in[slot], 16)
                sp.dma_start(dst[:, 3:7, :], rows[1].rearrange("(i r) d -> i r d", r=4)).then_inc(cache_in[slot], 16)
                by_class = rows[2].rearrange("(i v u r) d -> v r i u d", v=2, u=2, r=4)
                for r in range(4):
                    sp.dma_start(dst[32 * r:32 * r + 32, 1:3, :], by_class[0, r]).then_inc(cache_in[slot], 16)

            def late_values(h, b):
                sp.wait_ge(pv_used, 8 * h + b - 3)
                load_cache(h, cv, b)

            sp.dma_start(ident[:], c_id).then_inc(ident_in, 16)

            def frame(f, par):
                turns, t0 = turns_of(f)
                names = [n for _, n in turns]
                for u in range(SLOTS):
                    if isinstance(f, int) and f == 0 and u < 4:
                        load_x(u)
                    load(SLOTS * f + u, u, block_of(w_in, QB * (u % 4), frame_cols(f, u // 4)))
                    if isinstance(f, int) and f == 0:
                        continue
                    if u < 3 and not (isinstance(f, int) and f == 1):
                        late_values(f - 2, u + 5)
                    if u in (3, 4):
                        if not (isinstance(f, int) and f == 1):
                            sp.wait_ge(pv_used, 8 * (f - 2) + u + 2)
                        load_cache(f - 1, ck, u - 3)
                    if 8 <= u <= 18 and u % 2 == 0:
                        b = u // 2 - 2
                        sp.wait_ge(turned, t0 + names.index(("kt", b - 2, 1)) + 1)
                        load_cache(f - 1, ck, b)
                    if u in (19, 21):
                        b = 2 if u == 19 else 3
                        if not (isinstance(f, int) and f == 1):
                            sp.wait_ge(pv_used, 8 * (f - 1))
                        load_cache(f - 1, cv, b)
                    if u in (20, 22):
                        b = u // 2 - 10
                        sp.wait_ge(turned, t0 + names.index(("kt", 6 + b, 1)) + 1)
                        load_cache(f - 1, cv, b)
                    if u == 39:
                        late_values(f - 1, 4)
            frames(sp, frame)

            def gate_pair(i, first):
                for u in range(8):
                    col = (COL_U if u < 4 else COL_ZA) + P + i * P
                    load(Q_GATE + 8 * i + u, u, block_of(w_in, QB * (u % 4), col))
                    if first and u < 3:
                        late_values(HEADS - 1, u + 5)
            gate_pair(0, True)
            with sp.Fori(1, 7) as i:
                gate_pair(i, False)
            for q0, col0, w_o in ((Q_A, COL_GA, w_o_a), (Q_B, COL_GB, w_o_b)):
                with sp.Fori(0, 8) as i:
                    for u in range(12):
                        v, col = u % 6, i * (2 * P) + (u // 6) * P
                        src = block_of(w_in, QB * v, col + col0) if v < 4 else block_of(w_o, QB * (v - 4), col)
                        load(q0 + 12 * i + u, u, src)
            with sp.Fori(0, 16) as i:
                for u in range(4):
                    load(Q_OUT + 4 * i + u, u, block_of(w_out, QB * u, i * P))
            for by, n in ((o_norm_p, 0), (o_norm_v, 0), (o_norm_p, 1), (o_norm_v, 1), (o_norm_p, 2), (o_norm_p, 3),
                          (o_norm_v, 2), (o_norm_p, 4), (o_norm_v, 3), (o_norm_p, 5)):
                c, cols = n // 2 + (2 if by is o_norm_p else 0), half_cols(n % 2)
                dst = (y_prompt[0].rearrange("(i r) d -> r i d", r=4)[c] if c < 4
                       else y_sample.rearrange("b t d -> (b t) d"))
                sp.wait_ge(by, n + 1)
                sp.dma_start(dst[:, cols], res[0:tile_rows(c), c, cols]).then_inc(o_stored[c], 16)
            sp.wait_ge(k_stored, 32 * GROUPS * HEADS)
            sp.wait_ge(v_stored, 32 * GROUPS * HEADS)
            sp.wait_ge(gv_stored, 16)
            for c in range(5):
                sp.wait_ge(o_stored[c], 32)

        @block.gpsimd
        def _(pool):
            pool.dma_start(bn0[:], b_in[0, 0:P * P].rearrange("(c n) -> c n", n=P)).then_inc(b_loaded, 16)
            pool.dma_start(bn1[:], b_in[0, P * P:].rearrange("(c n) -> c n", n=P)).then_inc(b_loaded, 16)
            pool.wait_ge(x_loaded[3], 32)
            for dst, src in ((cos, c_cos), (sin, c_sin), (mask, c_mask), (smask, c_smask)):
                pool.dma_start(dst[:], src).then_inc(consts, 16)

            def frame(f, par):
                turns, t0 = turns_of(f)
                names = [n for _, n in turns]
                gmlp = isinstance(f, int) and f == 8

                def store(kind, g):
                    src = knat if kind == "k" else vN[par][g]
                    dst_p, dst_s = (nk_p, nk_s) if kind == "k" else (nv_p, nv_s)
                    stored = k_stored if kind == "k" else v_stored
                    pool.wait_ge(turn_read, t0 + names.index((kind, g, 1)) + 1)
                    if not (isinstance(f, int) and f == 0 and g == 0):
                        pool.wait_ge(stored, 32 * (GROUPS * f + g))
                    keep = dst_p[g].shape[2] // 4
                    pool.dma_start(dst_p[g][0, 0, :, ds(f, 1), :].rearrange("(i r) o d -> i r (o d)", r=4),
                                   src[P - keep:P, 0:4, :]).then_inc(stored, 16)
                    pool.dma_start(dst_s[g][0, :, :, ds(f, 1), :].rearrange("b t o d -> (b t) (o d)"),
                                   src[0:SAMP, 4, :]).then_inc(stored, 16)
                if not gmlp:
                    for g in range(GROUPS):
                        store("k", g)
                        store("v", g)
                else:
                    pool.wait_ge(k_stored, 32 * GROUPS * HEADS)
                    for j in range(8):
                        pool.wait_ge(acc_read, CHUNKS * f + j + 1)
                        if j > 0:
                            pool.wait_ge(turned, t0 + names.index(("va", j - 1, 0)) + 1)
                        pool.tensor_copy(knat[:, 0:4, :].rearrange("p c (r i) -> p c r i", r=4),
                                         stage[:, j % 2, 0:SEQ].rearrange("p (r c i) -> p c r i", r=4, c=4)
                                         ).then_inc(v_sorted, 1)
                if not (isinstance(f, int) and f == 0):
                    a = f - 1
                    pool.wait_ge(y_done, a + 1)
                    pool.dma_start(yb_d[ds(a, 1)].rearrange("o p c -> p (o c)"), yt[:]).then_inc(y_stored, 16)
            frames(pool, frame)
            pool.wait_ge(k_stored, 32 * GROUPS * HEADS)
            pool.wait_ge(v_stored, 32 * GROUPS * HEADS)
            pool.wait_ge(y_stored, 16 * HEADS)
            pool.dma_start(lnvg[:], ln_v_g.broadcast_to([P, WIDTH])).then_inc(lnv_in, 16)
            pool.dma_start(lnvb[:], ln_v_b.broadcast_to([P, WIDTH])).then_inc(lnv_in, 16)
            pool.memset(w8n[:], 0.0).then_inc(g_zero, 1)
            pool.dma_start(bsb[:], b_s.broadcast_to([P, 8, P])).then_inc(g_loaded, 16)
            pool.dma_start(tri[:], c_tri).then_inc(g_loaded, 16)
            pool.dma_start(tri8[:], c_tri8).then_inc(g_loaded, 16)
            for r in range(4):
                pool.dma_start(wsn[32 * r:32 * r + 32, :, :],
                               w_s[0].rearrange("g (i r) j -> r i g j", r=4)[r]).then_inc(g_loaded, 16)
            pool.wait_ge(g_zero, 1)
            for b in range(DEC_B):
                pool.dma_start(w8n[8 * b:8 * b + 8, :, 8 * b:8 * b + 8],
                               w_s[0, :, 0:8, 0:8].rearrange("g i j -> i g j")).then_inc(g_loaded, 16)
            pool.wait_ge(g_loaded, GATE_TABLES)
            pool.tensor_copy(wss[:].rearrange("p g (r j) -> p g r j", r=4),
                             wsn[:].rearrange("p g (j r) -> p g r j", r=4)).then_inc(w_sorted, 1)
            pool.wait_ge(v_norm, 5)
            pool.dma_start(n_gv[0].rearrange("b t d -> (b t) d"), vn[0:SAMP, 4, :]).then_inc(gv_stored, 16)
            pool.wait_ge(y_split, 8)
            pool.wait_ge(gv_stored, 16)
            pool.dma_start(ybraw[:], yb_d.rearrange("h p c -> p h c")).then_inc(yb_loaded, 16)
            pool.wait_ge(yb_split, 8)
            pool.wait_ge(merged, 32)
            pool.dma_start(lng[:], ln_g.broadcast_to([P, D])).then_inc(ln_in, 16)
            pool.dma_start(lnb[:], ln_b.broadcast_to([P, D])).then_inc(ln_in, 16)
            x_res = x_prompt[0].rearrange("(i r) d -> i r d", r=4)
            xs_res = x_sample.rearrange("b t d -> (b t) d")

            def residual(n, s):
                pool.dma_start(xn[:, s, 0:4, :], x_res[:, :, ds(n * P, P)]).then_inc(xn_in[s], 16)
                pool.dma_start(xn[0:SAMP, s, 4, :], xs_res[:, ds(n * P, P)]).then_inc(xn_in[s], 16)
            residual(0, 0)
            residual(1, 1)
            with pool.Fori(0, 7) as i:
                for s in range(2):
                    pool.wait_ge(out_read, 4 * i + 2 * s + 2)
                    residual(2 * i + s + 2, s)
            for n in range(6):
                c, cols = 2 + n // 2, half_cols(n % 2)
                t = res[0:tile_rows(c), c, cols]
                pool.wait_ge(o_gained, n + 1)
                pool.tensor_tensor(t, t, lnb[0:tile_rows(c), cols], ALU.add).then_inc(o_norm_p, 1)

        @block.tensor
        def _(pe):
            def quarter(q, u, ks, mh, ml, p, first, last):
                pe.wait_ge(w_split, q + 1)
                for n, k in enumerate(ks):
                    for t, (w, x) in enumerate(((wh, mh), (wh, ml), (wl, mh))):
                        for h in range(2):
                            done = pe.matmul(accv[p][:, h, :], w[:, u % 4, n, :], x[:, k, h * HALF:(h + 1) * HALF],
                                             start=(first and n == 0 and t == 0),
                                             stop=(last and n == QB - 1 and t == 2))
                done.then_inc(w_used, 1)

            def turn_blocks(f, t0, names, name, pairs):
                n = names.index(name)
                if n % 2 == 0 and (t0 + n > 0 if isinstance(t0, int) else name[0] != "pts"):
                    pe.wait_ge(turn_read, t0 + n)
                    if kt_before(names, n):
                        pe.wait_ge(kt_split, 16 * (f - 1) + kt_before(names, n))
                    if n and names[n - 1] == ("pts", 1):
                        pe.wait_ge(ps_split, f)
                bank = n % 2
                for cols, src, rows, width in pairs:
                    done = pe.transpose(turn[0:width, bank, cols:cols + rows], src, ident[0:rows, 0:rows])
                done.then_inc(turned, 1)

            def turn_x(c):
                pe.wait_ge(ident_in, 16)
                pe.wait_ge(x_loaded[c], 32)
                for k in range(QB * c, QB * c + QB):
                    if k >= 3:
                        pe.wait_ge(x_split, k - 2)
                    to = x_bank(k)
                    for r in range(4):
                        pe.transpose(to[:, r * P:(r + 1) * P], xn0[:, r, k * P:(k + 1) * P], ident[:])
                    pe.transpose(to[:, SEQ:TOK], xn0[0:SAMP, 4, k * P:(k + 1) * P],
                                 ident[0:SAMP, 0:SAMP]).then_inc(x_turned, 1)
            turn_x(0)
            pe.wait_ge(b_loaded, 32)
            pe.transpose(acc[:, 0, 0:P], bn0[:], ident[:])
            pe.transpose(acc[:, 0, P:P + 8], bn1[:], ident[0:8, 0:8]).then_inc(b_turned, 1)
            turn_x(1)
            pe.wait_ge(b_ready, 1)

            def frame(f, par):
                turns, t0 = turns_of(f)
                names = [n for _, n in turns]
                attends = not (isinstance(f, int) and f == 0)
                gmlp = isinstance(f, int) and f == 8
                old = 1 - par

                def bank_free(name):
                    if not (isinstance(f, int) and f == 1 and name == "cache"):
                        pe.wait_ge(score_read, score_no(f, name) - 1)

                def keys_turned(b):
                    pe.wait_ge(cache_in[b % 2], 96 * (6 * (f - 1) + b // 2 + 1))
                    for part, tiles in enumerate(((0, 1, 2), (3, 4, 5, 6))):
                        turn_blocks(f, t0, names, ("kt", b, part),
                                    [(n * P, cache[:, b % 2, t, :], P, P) for n, t in enumerate(tiles)])

                def cache_scores(b):
                    if b == 0:
                        bank_free("cache")
                        pe.wait_ge(q_spread, 2 * GROUPS * f)
                    pe.wait_ge(kt_split, 16 * (f - 1) + 2 * b + 2)
                    queries = slice(SAMP * b, SAMP * b + SAMP)
                    for g, c0, c1, at in ((0, 0, P, 0), (2, P, 3 * P, P), (1, 3 * P, CACHED, 4 * P)):
                        for t, (q, k) in enumerate(((qzh, kth), (qzh, ktl), (qzl, kth))):
                            done = pe.matmul(scp[0:SAMP, at:at + c1 - c0], q[:, g, queries], k[:, c0:c1],
                                             start=(b == 0 and g != 2 and t == 0), stop=(b == DEC_B - 1 and t == 2),
                                             skip_group_check=True)
                    done.then_inc(keys_used, 1)

                def new_scores():
                    bank_free("new")
                    for g in range(GROUPS):
                        done = pe.matmul(scp[0:SAMP, g * SAMP:(g + 1) * SAMP], qT[old][g][:, SEQ:TOK],
                                         kT[old][g][:, SEQ:TOK], start=True, stop=True)
                    done.then_inc(scored, 1)

                def prompt_scores(i):
                    bank_free(("qk", i))
                    cols = slice(i * P, (i + 1) * P)
                    pe.matmul(scp[:, 0:SEQ], qT[old][0][:, cols], kT[old][0][:, 0:SEQ], start=True, stop=True)
                    for g in (1, 2):
                        done = pe.matmul(scp[:, SEQ + (g - 1) * P:SEQ + g * P], qT[old][g][:, cols],
                                         kT[old][g][:, cols], start=True, stop=True)
                    done.then_inc(scored, 1)

                def prompt_out(i):
                    bank_free(("pv", i))
                    pe.wait_ge(turn_read, t0 + names.index(("pt", i, 1)) + 1)
                    for n in range(6):
                        g, tile = (0, n) if n < 4 else (n - 3, i)
                        done = pe.matmul(scp[:, 0:P], vN[old][g][:, tile, :], pt[:, n * P:(n + 1) * P],
                                         start=(n == 0), stop=(n == 5))
                    done.then_inc(scored, 1)

                def cached_out(b):
                    if b == 0:
                        bank_free("cached_pv")
                        pe.wait_ge(ps_split, f)
                    pe.wait_ge(v_split, 8 * (f - 1) + b + 1)
                    rows = slice(DEC_T * b, DEC_T * (b + 1))
                    for n in range(7):
                        hi, lo = vh[b % 2][:, n, :], vl[:, b % 4, n, :]
                        for t, (p, val) in enumerate(((psh, hi), (psh, lo), (psl, hi))):
                            done = pe.matmul(scp[0:DEC_T, b * P:(b + 1) * P], p[:, n, rows], val,
                                             start=(n == 0 and t == 0), stop=(n == 6 and t == 2))
                    done.then_inc(pv_used, 1)

                def sample_out():
                    bank_free("sample_out")
                    for g in range(GROUPS):
                        pe.matmul(scp[:, SEQ:SEQ + SAMP], vN[old][g][0:SAMP, 4, :], psn[:, g, :],
                                  start=(g == 0), stop=(g == GROUPS - 1))
                    for b in range(DEC_B):
                        done = pe.transpose(scp[:, DEC_T * b:DEC_T * (b + 1)], osm[:, b * P:(b + 1) * P],
                                            ident[0:DEC_T, 0:DEC_T])
                    done.then_inc(scored, 1)

                for s in range(SLOTS):
                    q = SLOTS * f + s
                    j = s // 4
                    if s % 4 == 0:
                        if not (isinstance(f, int) and f == 0 and j < 2):
                            pe.wait_ge(acc_read, CHUNKS * f + j - 1)
                    if isinstance(f, int) and f == 0 and s < 4:
                        pe.wait_ge(x_split, QB * (s + 1))
                    quarter(q, s, range(QB * (s % 4), QB * (s % 4) + QB), xh, xl, j % 2, s % 4 == 0, s % 4 == 3)
                    if isinstance(f, int) and f == 0 and s < 2:
                        turn_x(s + 2)
                    if attends:
                        if s % 2 == 0 and 2 <= s <= 16:
                            cache_scores(s // 2 - 1)
                        if s % 2 == 0 and s < 16:
                            keys_turned(s // 2)
                        if s == 17:
                            new_scores()
                        for i in range(4):
                            if s == slot_qk(i):
                                prompt_scores(i)
                            if s == slot_turn_p(i):
                                pe.wait_ge(normed, 5 * (f - 1) + i + 2)
                                for part in range(2):
                                    turn_blocks(f, t0, names, ("pt", i, part),
                                                [((n - 4 * part) * P, sc[:, n * P:(n + 1) * P], P, P)
                                                 for n in (range(4) if part == 0 else range(4, 6))])
                            if s == slot_pv(i):
                                prompt_out(i)
                        if s == slot_pv(3):
                            turn_blocks(f, t0, names, ("pts", 0),
                                        [(n * SAMP, ss[:, n * P:(n + 1) * P], SAMP, P) for n in range(7)])
                            turn_blocks(f, t0, names, ("pts", 1),
                                        [(g * SAMP, ss[:, CACHED + g * SAMP:CACHED + (g + 1) * SAMP], SAMP, SAMP)
                                         for g in range(GROUPS)])
                        for b in range(DEC_B):
                            if s == SLOT_PVS[b]:
                                cached_out(b)
                        if s == 39:
                            sample_out()
                    if not gmlp:
                        for g in range(GROUPS):
                            if s == SLOT_K[g]:
                                pe.wait_ge(roped, 2 * GROUPS * f + 2 * g + 2)
                                turn_blocks(f, t0, names, ("k", g, 0),
                                            [(c * P, kT[par][g][:, c * P:(c + 1) * P], P, P) for c in range(4)])
                                turn_blocks(f, t0, names, ("k", g, 1), [(0, kT[par][g][:, SEQ:TOK], P, SAMP)])
                            if s == SLOT_V[g]:
                                pe.wait_ge(acc_read, CHUNKS * f + 3 * g + 3)
                                src = stage[:, (3 * g + 2) % 2, :]
                                turn_blocks(f, t0, names, ("v", g, 0),
                                            [(c * P, src[:, c * P:(c + 1) * P], P, P) for c in range(4)])
                                turn_blocks(f, t0, names, ("v", g, 1), [(0, src[:, SEQ:TOK], P, SAMP)])
                    else:
                        for n in range(8):
                            if s == 4 * n + 5:
                                pe.wait_ge(acc_read, CHUNKS * f + n + 1)
                                pe.wait_ge(v_sorted, n + 1)
                                src = stage[:, n % 2, :]
                                turn_blocks(f, t0, names, ("va", n, 0), [(c * P, knat[:, c, :], P, P) for c in range(4)])
                                turn_blocks(f, t0, names, ("va", n, 1), [(0, src[:, SEQ:TOK], P, SAMP)])

            frames(pe, frame)

            def mix(g):
                pe.wait_ge(score_read, S_ATT + 3 + g)
                for c in range(4):
                    pe.matmul(scp[:, c * P:(c + 1) * P], vn[:, c, g * P:(g + 1) * P], wct[:, g, :],
                              start=True, stop=True)
                pe.matmul(scp[:, SEQ:SEQ + SAMP], vn[0:SAMP, 4, g * P:(g + 1) * P], w8[:, g, :],
                          start=True, stop=True).then_inc(scored, 1)

            def gate_pair(i, g):
                for s in range(8):
                    q = Q_GATE + 8 * i + s
                    if s % 4 == 0:
                        pe.wait_ge(acc_read, R_GATE + 2 * i + s // 4 - 1)
                    quarter(q, s, range(QB * (s % 4), QB * (s % 4) + QB), xh, xl, s // 4, s % 4 == 0, s % 4 == 3)
                    if i == 1 and s in (0, 2):
                        if s == 0:
                            pe.wait_ge(g_loaded, GATE_TABLES)
                            pe.wait_ge(w_sorted, 1)
                        pe.wait_ge(score_read, S_ATT + s // 2)
                        for n in range(4):
                            done = pe.transpose(scp[:, n * P:(n + 1) * P], wss[:, 2 * s + n, :], ident[:])
                        done.then_inc(scored, 1)
                    if (i, s) == (1, 4):
                        pe.wait_ge(score_read, S_ATT + 2)
                        for n in range(8):
                            done = pe.transpose(scp[0:SAMP, n * SAMP:(n + 1) * SAMP], w8n[:, n, :],
                                                ident[0:SAMP, 0:SAMP])
                        done.then_inc(scored, 1)
                    if g is not None and s == 6:
                        pe.wait_ge(v_norm, 5)
                        mix(g)
            for i in range(7):
                gate_pair(i, None if i == 0 else i - 1)

            def branch_pair(i, q0, r0, n_merged, first_a, first_b):
                for s in range(12):
                    q = q0 + 12 * i + s
                    half, v = s // 6, s % 6
                    if v == 0:
                        pe.wait_ge(acc_read, r0 + 2 * i + half - (1 if first_a and half == 0 else 0))
                    if v == 4:
                        if first_a and half == 0:
                            pe.wait_ge(acc_read, R_A)
                            pe.wait_ge(y_split, 8)
                        else:
                            pe.wait_ge(merged, n_merged + 2 * i + half)
                        if first_b and half == 0:
                            pe.wait_ge(yb_split, 8)
                    if v < 4:
                        quarter(q, s, range(QB * v, QB * v + QB), xh, xl, 0, v == 0, v == 3)
                    else:
                        quarter(q, s, range(QB * (v - 4), QB * (v - 4) + QB), yh, yl, 1, v == 4, v == 5)
                    if first_a and s < 2:
                        mix(6 + s)
            branch_pair(0, Q_A, R_A, 0, True, False)
            with pe.Fori(1, 8) as i:
                branch_pair(i, Q_A, R_A, 0, False, False)
            branch_pair(0, Q_B, R_B, 16, False, True)
            with pe.Fori(1, 8) as i:
                branch_pair(i, Q_B, R_B, 16, False, False)

            def out_turn(n, p):
                pe.wait_ge(acc_read, R_OUT + n + 1)
                for part in range(2):
                    if part == 0 and not (isinstance(n, int) and n == 0):
                        pe.wait_ge(out_read, 2 * n)
                    src = stage[:, p, :]
                    if part == 0:
                        for c in range(4):
                            done = pe.transpose(turn[:, 0, c * P:(c + 1) * P], src[:, c * P:(c + 1) * P], ident[:])
                    else:
                        done = pe.transpose(turn[0:SAMP, 1, 0:P], src[:, SEQ:TOK], ident[:])
                    done.then_inc(out_turned, 1)

            def out_pair(i, first):
                for s in range(8):
                    p = s // 4
                    if s % 4 == 0:
                        if first:
                            pe.wait_ge(acc_read, R_OUT) if p == 0 else pe.wait_ge(merged, 32)
                        else:
                            pe.wait_ge(acc_read, R_OUT + 2 * i + p - 1)
                    if first and p == 0:
                        pe.wait_ge(m_split, QB * (s + 1))
                    quarter(Q_OUT + 8 * i + s, s, range(QB * (s % 4), QB * (s % 4) + QB), xh, xl, p,
                            s % 4 == 0, s % 4 == 3)
                    if s % 4 == 1 and not (first and p == 0):
                        out_turn(2 * i + p - 1, 1 - p)
            out_pair(0, True)
            with pe.Fori(1, 8) as i:
                out_pair(i, False)
            out_turn(15, 1)

        @block.scalar
        def _(act):
            def rounded(c0, u):
                q = 4 * c0 + u
                act.wait_ge(w_loaded[u % 4], 16 * (c0 + u // 4 + 1))
                if not (isinstance(q, int) and q < 4):
                    act.wait_ge(w_used, q - 3)
                nc.scalar.activation(wh[:, u % 4, :, :], raw[:, u % 4, :, :], ACT.Copy).then_inc(w_round, 1)

            def ahead(c0, u):
                rounded(c0, u + LEAD)

            def read_acc(q_end, p, out, func, col):
                act.wait_ge(w_used, q_end)
                nc.scalar.activation(out.rearrange("p (h c) -> p h c", h=2), accv[p], func,
                                     bias=bias[:, ds(col, 1)]).then_inc(acc_read, 1)

            for k in range(KB):
                if k == QB:
                    act.wait_ge(b_turned, 1)
                    nc.scalar.activation(bias[:], acc[:, 0, 0:136], ACT.Copy).then_inc(b_ready, 1)
                act.wait_ge(x_turned, k + 1)
                nc.scalar.activation(xh[:, k, :], x_bank(k)[:, 0:TOK], ACT.Copy).then_inc(x_round, 1)
                if k % QB == QB - 1 and k // QB < LEAD:
                    rounded(0, k // QB)
            act.wait_ge(b_ready, 1)

            def frame(f, par):
                turns, t0 = turns_of(f)
                names = [n for _, n in turns]
                attends = not (isinstance(f, int) and f == 0)
                gmlp = isinstance(f, int) and f == 8

                def turn_out(n):
                    name = names[n]
                    bank = n % 2
                    act.wait_ge(turned, t0 + n + 1)
                    if name[0] == "kt":
                        b, part = name[1:]
                        if part == 0 and not (isinstance(f, int) and f == 1 and b == 0):
                            act.wait_ge(keys_used, 8 * (f - 1) + b)
                            if b == 0:
                                act.wait_ge(pv_used, 8 * (f - 1))
                        out, src = ((kth[:, 0:3 * P], turn[:, bank, 0:3 * P]) if part == 0
                                    else (kth[:, 3 * P:CACHED], turn[:, bank, :]))
                    elif name[0] == "pt":
                        i, part = name[1:]
                        if part == 0 and i > 0:
                            act.wait_ge(scored, signal_no(f, ("pv", i - 1)))
                        out, src = ((pt[:, 0:4 * P], turn[:, bank, :]) if part == 0
                                    else (pt[:, 4 * P:6 * P], turn[:, bank, 0:2 * P]))
                    elif name[0] == "pts":
                        out, src = ((psh[:], turn[:, bank, 0:7 * SAMP].rearrange("p (n c) -> p n c", n=7))
                                    if name[1] == 0 else (psn[:], turn[0:SAMP, bank, 0:NEW]
                                                          .rearrange("p (n c) -> p n c", n=GROUPS)))
                    elif name[0] in ("k", "v"):
                        g, part = name[1:]
                        dst = knat if name[0] == "k" else vN[par][g]
                        if part == 0:
                            if name[0] == "k" and not (isinstance(f, int) and f == 0 and g == 0):
                                act.wait_ge(k_stored, 32 * (GROUPS * f + g))
                            if name[0] == "v" and attends:
                                act.wait_ge(v_stored, 32 * (GROUPS * (f - 1) + g))
                        out, src = ((dst[:, 0:4, :], turn[:, bank, :]) if part == 0
                                    else (dst[0:SAMP, 4, :], turn[0:SAMP, bank, 0:P]))
                    else:
                        n_, part = name[1:]
                        if n_ == 0 and part == 0:
                            act.wait_ge(v_stored, 32 * GROUPS * 7)
                        cols = slice(n_ * P, (n_ + 1) * P)
                        out, src = ((vn[:, 0:4, cols], turn[:, bank, :].rearrange("p (c d) -> p c d", c=4)) if part == 0
                                    else (vn[0:SAMP, 4, cols], turn[0:SAMP, bank, 0:P]))
                    nc.scalar.activation(out, src, ACT.Copy).then_inc(turn_read, 1)

                def round_values(b):
                    slot = b % 4
                    use = 6 * (f - 1) + (4 if b < 4 else 5) + 1 if slot < 2 else 2 * (f - 1) + b // 4 + 1
                    act.wait_ge(cache_in[slot], 96 * use)
                    if b == 0:
                        act.wait_ge(turned, t0 + names.index(("pt", 3, 1)) + 1)
                    elif b == 1:
                        act.wait_ge(scored, signal_no(f, ("pv", 3)))
                    else:
                        act.wait_ge(pv_used, 8 * (f - 1) + b - 1)
                    nc.scalar.activation(vh[b % 2][:], cache[:, slot, :, :], ACT.Copy).then_inc(v_round, 1)

                for s in range(SLOTS):
                    q = SLOTS * f + s
                    ahead(CHUNKS * f, s)
                    j = s // 4 - 1
                    if s % 4 == 0 and j < 0 and attends:
                        if not (isinstance(f, int) and f == 1):
                            act.wait_ge(y_done, f - 1)
                        read_acc(q, 1, zt[:], ACT.Silu, COL_ZB // P + f - 1)
                    if s % 4 == 0 and j >= 0:
                        if not gmlp:
                            if j == 0 and attends:
                                act.wait_ge(turned, t0)
                            if j == 1 and attends:
                                act.wait_ge(roped, 2 * GROUPS * f)
                            if j in (2, 3, 5, 6, 8):
                                act.wait_ge(roped, 2 * GROUPS * f + {2: 1, 3: 2, 5: 3, 6: 4, 8: 5}[j])
                            if j in (4, 7):
                                act.wait_ge(turned, t0 + names.index(("v", j // 3 - 1, 1)) + 1)
                        else:
                            act.wait_ge(turned, t0) if j < 2 else act.wait_ge(turned, t0 + names.index(("va", j - 2, 1)) + 1)
                            if j == 1:
                                act.wait_ge(roped, 2 * GROUPS * HEADS)
                        func = ACT.Gelu if gmlp else ACT.Identity
                        col = frame_cols(f, j)
                        cb = col // P if isinstance(col, int) else frame_cols(0, j) // P + f
                        read_acc(q, j % 2, stage[:, j % 2, :], func, cb)
                    for n, (at, name) in enumerate(turns):
                        if at == s - 1:
                            turn_out(n)
                    if attends:
                        for b in range(DEC_B):
                            if s == SLOT_VS[b]:
                                round_values(b)
                        if s == 18:
                            act.wait_ge(biased, 5 * (f - 1) + 1)
                            nc.scalar.activation(ss[:], ss[:], ACT.Exp, bias=small[0:SAMP, 4:5],
                                                 accum_out=small[0:SAMP, 5:6]).then_inc(expd, 1)
                        for i in range(4):
                            if s == slot_qk(i) + 1:
                                act.wait_ge(biased, 5 * (f - 1) + i + 2)
                                nc.scalar.activation(sc[:], sc[:], ACT.Exp, bias=small[:, 19:20],
                                                     accum_out=small[:, 20:21]).then_inc(expd, 1)

            frames(act, frame)

            def gate_pair(i, g):
                for s in range(8):
                    q = Q_GATE + 8 * i + s
                    ahead(Q_GATE // 4 + 2 * i, s)
                    if s == 0:
                        if g is None:
                            act.wait_ge(turned, TURNS_ALL)
                        else:
                            act.wait_ge(gated, i)
                        read_acc(q, 1, stage[:, 1, :], ACT.Silu, COL_ZA // P + i)
                    if s == 1 and g is None:
                        act.wait_ge(v_var, 1)
                        nc.scalar.activation(vmv[:, :, 1], vmv[:, :, 1], ACT.Sqrt).then_inc(v_sqrt, 1)
                    if s == 4:
                        act.wait_ge(gated, i + 1)
                        read_acc(q, 0, stage[:, 0, :], ACT.Gelu, COL_U // P + i + 1)
                    if s == 7 and g is not None:
                        y_rounded(g)

            def y_rounded(g):
                act.wait_ge(y_ready, g + 1)
                nc.scalar.activation(yh[:, ds(g, 1), :], ym[:], ACT.Copy).then_inc(y_round, 1)
            gate_pair(0, None)
            with act.Fori(1, 7) as i:
                gate_pair(i, i - 1)

            def round_merged(quarter):
                for k in range(QB * quarter, QB * quarter + QB):
                    if k >= KB - 2:
                        act.wait_ge(merged, KB + k + 1)
                    nc.scalar.activation(xh[:, k, :], m[:, k, :], ACT.Copy).then_inc(m_round, 1)

            def branch_pair(i, q0, r0, n_merged, col0, first_a, first_b):
                for s in range(12):
                    q = q0 + 12 * i + s
                    ahead(q0 // 4 + 3 * i, s)
                    if first_a and s == 0:
                        act.wait_ge(gated, 7)
                        read_acc(q, 1, stage[:, 1, :], ACT.Silu, COL_ZA // P + 7)
                    if first_a and 1 <= s < 3:
                        y_rounded(s + 5)
                    if first_b and s < 4:
                        if s == 0:
                            act.wait_ge(yb_loaded, 16)
                            act.wait_ge(w_used, Q_B)
                        for h in (2 * s, 2 * s + 1):
                            nc.scalar.activation(yh[:, h, :], ybraw[:, h, :], ACT.Copy).then_inc(yb_round, 1)
                    if s in (4, 10):
                        half = s // 6
                        if first_a:
                            act.wait_ge(gated, 8)
                        else:
                            act.wait_ge(merged, n_merged + 2 * i + half - 1)
                        read_acc(q, 0, stage[:, half, :], ACT.Sigmoid, 2 * i + half + col0 // P)
                    if isinstance(i, int) and i == 7 and s >= 10:
                        if s == 10:
                            act.wait_ge(w_used, Q_OUT - 2)
                        round_merged(s - 10)
            branch_pair(0, Q_A, R_A, 0, COL_GA, True, False)
            with act.Fori(1, 8) as i:
                branch_pair(i, Q_A, R_A, 0, COL_GA, False, False)
            branch_pair(0, Q_B, R_B, 16, COL_GB, False, True)
            with act.Fori(1, 7) as i:
                branch_pair(i, Q_B, R_B, 16, COL_GB, False, False)
            branch_pair(7, Q_B, R_B, 16, COL_GB, False, False)

            def read_out(n, q_end, p):
                act.wait_ge(w_used, q_end)
                if isinstance(n, int) and n == 0:
                    act.wait_ge(merged, 32)
                else:
                    act.wait_ge(out_turned, 2 * n)
                nc.scalar.activation(stage[:, p, :].rearrange("p (h c) -> p h c", h=2), accv[p],
                                     ACT.Copy).then_inc(acc_read, 1)

            def out_pair(i, first, last):
                for s in range(8):
                    q = Q_OUT + 8 * i + s
                    if not last or s + LEAD < 8:
                        ahead(Q_OUT // 4 + 2 * i, s)
                    if first and s < 2:
                        round_merged(s + 2)
                    if s % 4 == 0 and not (first and s == 0):
                        p = 1 - s // 4
                        read_out(2 * i + s // 4 - 1, q, p)
            out_pair(0, True, False)
            with act.Fori(1, 7) as i:
                out_pair(i, False, False)
            out_pair(7, False, True)
            read_out(15, Q_END, 1)
            act.wait_ge(o_var, 1)
            nc.scalar.activation(rmv[:, :, 1], rmv[:, :, 1], ACT.Sqrt).then_inc(o_sqrt, 1)
            for n in range(6):
                c, cols = 2 + n // 2, half_cols(n % 2)
                t = res[0:tile_rows(c), c, cols]
                act.wait_ge(o_var, 2)
                nc.scalar.activation(t, t, ACT.Identity, bias=shift[0:tile_rows(c), c:c + 1],
                                     scale=rmv[0:tile_rows(c), c, 1:2]).then_inc(o_scaled, 1)

        @block.vector
        def _(dve):
            v = nc.vector

            class Links:
                base, n = 0, 0

                def mark(self, ins):
                    self.n += 1
                    ins.then_inc(vector_done, 1)

                def then(self, ins):
                    self.mark(ins)
                    self.wait()

                def wait(self):
                    dve.wait_ge(vector_done, self.base + self.n)
            links = Links()

            def split(q, u):
                dve.wait_ge(w_round, q + 1)
                v.tensor_tensor(wl[:, u % 4, :, :], raw[:, u % 4, :, :], wh[:, u % 4, :, :].bitcast(F32),
                                ALU.subtract).then_inc(w_split, 1)

            def ahead(q, u):
                split(q + LEAD, u + LEAD)

            v.memset(qzh[:].bitcast(F32), 0.0).then_inc(zeroed, 1)
            v.memset(qzl[:].bitcast(F32), 0.0).then_inc(zeroed, 1)
            for k in range(KB):
                dve.wait_ge(x_round, k + 1)
                v.tensor_tensor(xl[:, k, :], x_bank(k)[:, 0:TOK], xh[:, k, :].bitcast(F32),
                                ALU.subtract).then_inc(x_split, 1)
                if k % QB == QB - 1 and k // QB < LEAD:
                    split(k // QB, k // QB)
            dve.wait_ge(consts, 16 * 4)
            dve.wait_ge(zeroed, 2)

            def frame(f, par):
                attends = not (isinstance(f, int) and f == 0)
                gmlp = isinstance(f, int) and f == 8
                turns, t0 = turns_of(f)
                names = [n for _, n in turns]
                links.n = 0
                links.base = 0 if not attends else CHAIN_FIRST + CHAIN_HEAD * (f - 1)

                def split_keys(b):
                    for part, c0, c1 in ((0, 0, 3 * P), (1, 3 * P, CACHED)):
                        n = names.index(("kt", b, part))
                        dve.wait_ge(turn_read, t0 + n + 1)
                        v.tensor_tensor(ktl[:, c0:c1], turn[:, n % 2, 0:c1 - c0], kth[:, c0:c1].bitcast(F32),
                                        ALU.subtract).then_inc(kt_split, 1)

                def rope_rows(j):
                    st = stage[:, j % 2, :]
                    dve.wait_ge(acc_read, CHUNKS * f + j + 1)
                    if not (isinstance(f, int) and f == 0 and j == 0):
                        dve.wait_ge(roped, 2 * GROUPS * f + 2 * (j // 3) + j % 3)
                    links.mark(v.tensor_tensor(rot[0:64, :], st[64:P, :], sin[64:P, :], ALU.mult))
                    links.then(v.tensor_tensor(rot[64:P, :], st[0:64, :], sin[0:64, :], ALU.mult))

                def rope_sum(j):
                    st = stage[:, j % 2, :]
                    dst = (qT if j % 3 == 0 else kT)[par][j // 3]
                    links.then(v.tensor_tensor(dst, st, cos[:], ALU.mult))
                    v.tensor_tensor(dst, dst, rot[:], ALU.add).then_inc(roped, 1)

                def negate(rows, c):
                    v.tensor_scalar(small[0:rows, c:c + 1], small[0:rows, c - 1:c], -1.0, None,
                                    ALU.mult).then_inc(biased, 1)

                def normalise(tile, rows, c):
                    links.then(v.reciprocal(small[0:rows, c + 1:c + 2], small[0:rows, c:c + 1]))
                    v.tensor_scalar(tile, tile, small[0:rows, c + 1:c + 2], None, ALU.mult).then_inc(normed, 1)

                def masked(out, scores, add, top):
                    return v.tensor_tensor_reduce(out, scores, add, SCALE, MASKED, ALU.add, ALU.max, top)

                for s in range(SLOTS):
                    q = SLOTS * f + s
                    if attends and s == 17:
                        dve.wait_ge(keys_used, DEC_B * f)
                    if attends and s == 18:
                        dve.wait_ge(scored, signal_no(f, "new"))
                    for i in range(4):
                        if attends and s == slot_qk(i) + 1:
                            if i > 0:
                                dve.wait_ge(turned, t0 + names.index(("pt", i - 1, 1)) + 1)
                            dve.wait_ge(scored, signal_no(f, ("qk", i)))
                    ahead(q, s)
                    if attends:
                        if s % 2 == 1 and s < 16:
                            split_keys(s // 2)
                        if s == 17:
                            links.mark(masked(ss[:, 0:3 * P], scp[0:SAMP, 0:3 * P], smask[:, 0:3 * P],
                                              small[0:SAMP, 0:1]))
                            masked(ss[:, 3 * P:CACHED], scp[0:SAMP, SEQ:2 * SEQ], smask[:, 3 * P:CACHED],
                                   small[0:SAMP, 1:2]).then_inc(score_read, 1)
                        if s == 18:
                            masked(ss[:, CACHED:], scp[0:SAMP, 0:NEW], smask[:, CACHED:],
                                   small[0:SAMP, 2:3]).then_inc(score_read, 1)
                            links.wait()
                            dve.wait_ge(score_read, score_no(f, "new"))
                            links.then(v.tensor_reduce(small[0:SAMP, 3:4], small[0:SAMP, 0:3],
                                                       mybir.AxisListType.X, ALU.max))
                            negate(SAMP, 4)
                        if s == 19:
                            dve.wait_ge(expd, 5 * (f - 1) + 1)
                            normalise(ss[:], SAMP, 5)
                        for i in range(4):
                            if s == slot_qk(i) + 1:
                                links.mark(masked(sc[:, 0:SEQ], scp[:, 0:SEQ], mask[:, (3 - i) * P:(7 - i) * P],
                                                  small[:, 16:17]))
                                masked(sc[:, SEQ:], scp[:, SEQ:SEQ + 2 * P], mask[:, 7 * P:],
                                       small[:, 17:18]).then_inc(score_read, 1)
                                links.wait()
                                dve.wait_ge(score_read, score_no(f, ("qk", i)))
                                links.then(v.tensor_tensor(small[:, 18:19], small[:, 16:17], small[:, 17:18], ALU.max))
                                negate(P, 19)
                            if s == slot_turn_p(i):
                                dve.wait_ge(expd, 5 * (f - 1) + i + 2)
                                normalise(sc[:], P, 20)
                            if s == slot_pv(i) + 1:
                                if i == 0:
                                    dve.wait_ge(acc_read, CHUNKS * f)
                                    if not (isinstance(f, int) and f == 1):
                                        dve.wait_ge(y_stored, 16 * (f - 1))
                                dve.wait_ge(scored, signal_no(f, ("pv", i)))
                                cols = slice(i * P, (i + 1) * P)
                                v.tensor_tensor(yt[:, cols], scp[:, 0:P], zt[:, cols], ALU.mult).then_inc(score_read, 1)
                        if s == 32:
                            n = names.index(("pts", 0))
                            dve.wait_ge(turn_read, t0 + n + 2)
                            v.tensor_tensor(psl[:], turn[:, n % 2, 0:7 * SAMP].rearrange("p (n c) -> p n c", n=7),
                                            psh[:].bitcast(F32), ALU.subtract).then_inc(ps_split, 1)
                        for b in range(DEC_B):
                            if s == SLOT_VS[b]:
                                dve.wait_ge(v_round, 8 * (f - 1) + b + 1)
                                v.tensor_tensor(vl[:, b % 4, :, :], cache[:, b % 4, :, :],
                                                vh[b % 2][:].bitcast(F32), ALU.subtract).then_inc(v_split, 1)
                        if s == 39:
                            dve.wait_ge(pv_used, 8 * f)
                            v.tensor_copy(osm[:], scp[0:DEC_T, :]).then_inc(score_read, 1)
                            dve.wait_ge(scored, signal_no(f, "sample_out"))
                            links.then(v.tensor_copy(otmp[:], scp[:, SEQ:SEQ + SAMP]))
                            v.tensor_tensor(otmp[:], otmp[:], scp[:, 0:SAMP], ALU.add).then_inc(score_read, 1)
                            dve.wait_ge(score_read, score_no(f, "sample_out"))
                            v.tensor_tensor(yt[:, SEQ:TOK], otmp[:], zt[:, SEQ:TOK], ALU.mult).then_inc(y_done, 1)
                    if not gmlp:
                        for j in (0, 1, 3, 4, 6, 7):
                            if s == 4 * j + 5:
                                rope_rows(j)
                            if s == 4 * j + 6:
                                rope_sum(j)
                        if s == 38:
                            dve.wait_ge(roped, 2 * GROUPS * f + 2 * GROUPS)
                            own = lambda z, g: z[:, g, :].rearrange("p (b c) -> p b c", c=SAMP + DEC_T)[:, :, 0:DEC_T]
                            for half in range(2):
                                for g in range(GROUPS):
                                    src = qT[par][g][:, SEQ:TOK].rearrange("p (b t) -> p b t", b=DEC_B)
                                    if half == 0:
                                        v.tensor_copy(own(qzh, g), src).then_inc(q_spread, 1)
                                    else:
                                        v.tensor_tensor(own(qzl, g), src, own(qzh, g).bitcast(F32),
                                                        ALU.subtract).then_inc(q_spread, 1)
                                if half == 0:
                                    dve.wait_ge(q_spread, 2 * GROUPS * f + GROUPS)
                    elif s >= 35:
                        c = s - 35
                        if c == 0:
                            dve.wait_ge(turn_read, TURNS_ALL)
                            links.then(v.memset(vmv[:], 1.0))
                        rows = P if c < 4 else SAMP
                        for h in range(2):
                            links.then(v.bn_stats(vstat[0:rows, c, h, :], vn[0:rows, c, h * 512:(h + 1) * 512]))
                quota = CHAIN_FIRST if not attends else CHAIN_HEAD
                if not gmlp:
                    assert links.n == quota, (links.n, quota)

            frames(dve, frame)

            def mixed(g):
                dve.wait_ge(scored, S_SIG + 3 + g + 1)
                if not (isinstance(g, int) and g == 0):
                    dve.wait_ge(y_split, g)
                bs = bsb[:, ds(g, 1), :]
                v.tensor_tensor(ym[:, 0:SEQ].rearrange("p (r c i) -> p r c i", r=4, c=4),
                                scp[:, 0:SEQ].rearrange("p (c r i) -> p r c i", c=4, r=4),
                                bs.rearrange("p o (i r) -> p r o i", r=4).broadcast_to([P, 4, 4, 32]),
                                ALU.add).then_inc(y_mixed, 1)
                v.tensor_tensor(ym[:, SEQ:TOK].rearrange("p (b t) -> p b t", b=DEC_B),
                                scp[:, SEQ:SEQ + SAMP].rearrange("p (b t) -> p b t", b=DEC_B),
                                bs[:, :, 0:DEC_T].broadcast_to([P, DEC_B, DEC_T]), ALU.add).then_inc(score_read, 1)
                dve.wait_ge(y_mixed, g + 1)
                dve.wait_ge(score_read, S_ATT + 3 + g + 1)
                v.tensor_tensor(ym[:], ym[:], tg[:, ds(g, 1), :], ALU.mult).then_inc(y_ready, 1)

            def y_rest(g):
                dve.wait_ge(y_ready, g + 1)
                dve.wait_ge(y_round, g + 1)
                v.tensor_tensor(yl[:, ds(g, 1), :], ym[:], yh[:, ds(g, 1), :].bitcast(F32),
                                ALU.subtract).then_inc(y_split, 1)

            def normalise_v(c):
                rows = P if c < 4 else SAMP
                t = vn[0:rows, c, :]
                links.then(v.scalar_tensor_tensor(out=t, in0=t, scalar=vmv[0:rows, c, 0:1], in1=lnvg[0:rows, :],
                                                  op0=ALU.subtract, op1=ALU.mult))
                v.scalar_tensor_tensor(out=t, in0=t, scalar=vmv[0:rows, c, 1:2], in1=lnvb[0:rows, :],
                                       op0=ALU.mult, op1=ALU.add).then_inc(v_norm, 1)

            links.base, links.n = links.base + links.n, 0
            for s in range(8):
                ahead(Q_GATE + s, s)
                if s == 0:
                    for c in range(5):
                        rows = P if c < 4 else SAMP
                        links.mark(v.bn_aggr(vmv[0:rows, c, :], vstat[0:rows, c, :, :].rearrange("p h s -> p (h s)")))
                    links.wait()
                    v.tensor_scalar(vmv[:, :, 1], vmv[:, :, 1], LN_EPS, None, ALU.add).then_inc(v_var, 1)
                if s == 1:
                    dve.wait_ge(g_zero, 1)
                    dve.wait_ge(acc_read, R_GATE)
                    v.tensor_tensor(tg[:, 0, :], stage[:, 0, :], stage[:, 1, :], ALU.mult).then_inc(gated, 1)
                if s == 2:
                    dve.wait_ge(v_sqrt, 1)
                    links.then(v.reciprocal(vmv[:, :, 1], vmv[:, :, 1]))
                    dve.wait_ge(lnv_in, 16 * 2)
                if s >= 3:
                    normalise_v(s - 3)

            def gate_pair(i, g):
                for s in range(8):
                    ahead(Q_GATE + 8 * i + s, s)
                    if s in (1, 3) and isinstance(g, int):
                        dve.wait_ge(g_loaded, GATE_TABLES)
                        dve.wait_ge(scored, S_SIG + s // 2 + 1)
                        v.tensor_tensor(wct[:, 2 * s - 2:2 * s + 2, :], scp[:, 0:SEQ].rearrange("p (g i) -> p g i", g=4),
                                        tri[:].rearrange("p (o i) -> p o i", o=1).broadcast_to([P, 4, P]),
                                        ALU.mult).then_inc(score_read, 1)
                    if s == 0 and not isinstance(g, int):
                        y_rest(g - 1)
                    if s == 5 and isinstance(g, int):
                        dve.wait_ge(scored, S_SIG + 3)
                        v.tensor_tensor(w8[:], scp[0:SAMP, 0:8 * SAMP].rearrange("p (g i) -> p g i", g=8),
                                        tri8[:].rearrange("p (o i) -> p o i", o=1).broadcast_to([SAMP, 8, SAMP]),
                                        ALU.mult).then_inc(score_read, 1)
                    if s == 1:
                        dve.wait_ge(acc_read, R_GATE + 2 * i)
                        v.tensor_tensor(tg[:, ds(i, 1), :], stage[:, 0, :], stage[:, 1, :],
                                        ALU.mult).then_inc(gated, 1)
                    if s == 7:
                        mixed(g)
            gate_pair(1, 0)
            with dve.Fori(2, 7) as i:
                gate_pair(i, i - 1)

            def merge(n, half, count):
                dve.wait_ge(acc_read, (R_A if count == 0 else R_B) + n + 1)
                dve.wait_ge(w_used, (Q_A if count == 0 else Q_B) + 6 * n + 6)
                prod = accv[1]
                g2 = stage[:, half, :].rearrange("p (h c) -> p h c", h=2)
                if count == 0:
                    v.tensor_tensor(m[:, ds(n, 1), :].rearrange("p o (h c) -> p (o h) c", h=2), prod, g2,
                                    ALU.mult).then_inc(merged, 1)
                else:
                    v.tensor_tensor(mtmp[:].rearrange("p (h c) -> p h c", h=2), prod, g2,
                                    ALU.mult).then_inc(b_product, 1)
                    dve.wait_ge(b_product, n + 1)
                    mt = m[:, ds(n, 1), :]
                    v.tensor_tensor(mt, mt, mtmp[:], ALU.add).then_inc(merged, 1)

            def split_merged(quarter):
                for k in range(QB * quarter, QB * quarter + QB):
                    dve.wait_ge(m_round, k + 1)
                    v.tensor_tensor(xl[:, k, :], m[:, k, :], xh[:, k, :].bitcast(F32),
                                    ALU.subtract).then_inc(m_split, 1)

            def branch_pair(i, q0, count, first_a, first_b):
                for s in range(12):
                    ahead(q0 + 12 * i + s, s)
                    if first_a:
                        if s == 0:
                            y_rest(5)
                        if s == 1:
                            mixed(6)
                        if s == 2:
                            dve.wait_ge(acc_read, R_A)
                            v.tensor_tensor(tg[:, 7, :], stage[:, 0, :], stage[:, 1, :], ALU.mult).then_inc(gated, 1)
                            y_rest(6)
                            dve.wait_ge(gated, 8)
                            mixed(7)
                        if s == 3:
                            y_rest(7)
                    elif s == 0:
                        merge(15, 1, 0) if first_b else merge(2 * i - 1, 1, count)
                    if first_b and s < 4:
                        for h in (2 * s, 2 * s + 1):
                            dve.wait_ge(yb_round, h + 1)
                            v.tensor_tensor(yl[:, h, :], ybraw[:, h, :], yh[:, h, :].bitcast(F32),
                                            ALU.subtract).then_inc(yb_split, 1)
                    if s == 6:
                        merge(2 * i, 0, count)
                    if count and isinstance(i, int) and i == 7 and s >= 10:
                        split_merged(s - 10)
            branch_pair(0, Q_A, 0, True, False)
            with dve.Fori(1, 8) as i:
                branch_pair(i, Q_A, 0, False, False)
            branch_pair(0, Q_B, 16, False, True)
            with dve.Fori(1, 7) as i:
                branch_pair(i, Q_B, 16, False, False)
            branch_pair(7, Q_B, 16, False, False)

            def residual(n, p, uses):
                dve.wait_ge(xn_in[p], 32 * uses)
                for part, (rows, c0, c1) in enumerate(((P, 0, 4), (SAMP, 4, 5))):
                    dve.wait_ge(out_turned, 2 * n + part + 1)
                    v.scalar_tensor_tensor(out=res[0:rows, c0:c1, ds(n * P, P)], in0=xn[0:rows, p, c0:c1, :],
                                           scalar=ALPHA, in1=turn[0:rows, part, 0:(c1 - c0) * P]
                                           .rearrange("p (c d) -> p c d", d=P),
                                           op0=ALU.mult, op1=ALU.add).then_inc(out_read, 1)

            def statistics(n):
                dve.wait_ge(out_read, 2 * n + 2)
                for c in range(5):
                    rows = P if c < 4 else SAMP
                    v.bn_stats(rstat[0:rows, c, ds(n, 1), :], res[0:rows, c, ds(n * P, P)]).then_inc(o_stats, 1)

            def out_pair(i, first, last):
                for s in range(8):
                    if first and s == 0:
                        merge(15, 1, 16)
                    if not last or s + LEAD < 8:
                        ahead(Q_OUT + 8 * i + s, s)
                    if first and s < 2:
                        split_merged(s + 2)
                    n, p = 2 * i + s // 4 - 1, 1 - s // 4
                    if not (first and s < 4):
                        if s % 4 == 2:
                            residual(n, p, i if s < 4 else i + 1)
                        if s % 4 == 3:
                            statistics(n)
            out_pair(0, True, False)
            with dve.Fori(1, 7) as i:
                out_pair(i, False, False)
            out_pair(7, False, True)
            residual(15, 1, 8)
            links.base, links.n = links.base + links.n, 0
            statistics(15)
            dve.wait_ge(o_stats, 5 * KB)
            links.then(v.memset(rmv[:], 1.0))
            for c in range(5):
                rows = P if c < 4 else SAMP
                links.mark(v.bn_aggr(rmv[0:rows, c, :], rstat[0:rows, c, :, :].rearrange("p h s -> p (h s)")))
            links.wait()
            v.tensor_scalar(rmv[:, :, 1], rmv[:, :, 1], LN_EPS, None, ALU.add).then_inc(o_var, 1)
            dve.wait_ge(o_sqrt, 1)
            links.then(v.reciprocal(rmv[:, :, 1], rmv[:, :, 1]))
            v.scalar_tensor_tensor(out=shift[:], in0=rmv[:, :, 0], scalar=-1.0, in1=rmv[:, :, 1],
                                   op0=ALU.mult, op1=ALU.mult).then_inc(o_var, 1)
            dve.wait_ge(ln_in, 32)

            def gain(n):
                c, cols = 2 + n // 2, half_cols(n % 2)
                t = res[0:tile_rows(c), c, cols]
                dve.wait_ge(o_scaled, n + 1)
                v.tensor_tensor(t, t, lng[0:tile_rows(c), cols], ALU.mult).then_inc(o_gained, 1)

            def centred(n):
                c, cols = n // 2, half_cols(n % 2)
                t = res[0:P, c, cols]
                v.scalar_tensor_tensor(out=t, in0=t, scalar=rmv[:, c, 0:1], in1=lng[:, cols],
                                       op0=ALU.subtract, op1=ALU.mult).then_inc(o_centred, 1)

            def scaled(n):
                c, cols = n // 2, half_cols(n % 2)
                t = res[0:P, c, cols]
                dve.wait_ge(o_centred, n + 1)
                v.scalar_tensor_tensor(out=t, in0=t, scalar=rmv[:, c, 1:2], in1=lnb[:, cols],
                                       op0=ALU.mult, op1=ALU.add).then_inc(o_norm_v, 1)

            for step, n in ((centred, 0), (gain, 0), (gain, 1), (scaled, 0), (gain, 2), (centred, 1), (scaled, 1),
                            (gain, 3), (centred, 2), (scaled, 2), (gain, 4), (gain, 5), (centred, 3), (scaled, 3)):
                step(n)


def tables():
    i, r = np.meshgrid(np.arange(P), np.arange(4), indexing="ij")
    prompt = (4 * i + r).T.reshape(-1)
    sample = PAST + np.tile(np.arange(DEC_T), DEC_B)
    pos = np.concatenate([prompt, sample]).astype(np.float32)
    inv = np.float32(10000.0) ** (-np.arange(64, dtype=np.float32) * np.float32(2.0) / np.float32(P))
    ang = (pos[None, :] * inv[:, None].astype(np.float32)).astype(np.float32)
    cos, sin = np.cos(ang).astype(np.float32), np.sin(ang).astype(np.float32)
    gap = np.arange(P)[:, None] - np.arange(P)[None, :]
    below, equal, above = ((gap >= 0) & (gap <= 31)), ((gap >= 0) & (gap <= 32)), ((gap >= 1) & (gap <= 32))
    far = np.where(gap >= 0, True, False)
    strip = [below] * 3 + [equal] + [above] * 3 + [far, far & (gap % 4 == 0)]
    mask = np.where(np.concatenate(strip, 1), 0.0, MASKED).astype(np.float32)
    t = np.tile(np.arange(DEC_T), DEC_B)[:, None]
    b = np.repeat(np.arange(DEC_B), DEC_T)[:, None]
    p = np.arange(P)[None, :]
    seen = [p >= t]
    for u in range(2):
        n = 16 * (p % 32) + 4 * u + p // 32
        seen.append((n % 16 == t) & (n >= t))
    for k in range(4):
        n = 4 * p + k
        seen.append((n % 4 == t % 4) & (n >= t))
    for dil in (1, 4, 16):
        seen.append((b == b.T) & (t >= t.T) & ((t - t.T) % dil == 0))
    smask = np.where(np.concatenate(seen, 1), 0.0, MASKED).astype(np.float32)
    at = np.arange(P) % 32 * 4 + np.arange(P) // 32
    tri = (at[:, None] <= at[None, :]).astype(np.float32)
    tri8 = ((b == b.T) & (t <= t.T)).astype(np.float32)
    return (np.concatenate([cos, cos], 0), np.concatenate([sin, -sin], 0), mask, smask, tri, tri8,
            np.eye(P, dtype=np.float32))


_INS = ["x_prompt", "x_sample", "cache_k_w128", "cache_k_w512", "cache_k_w2048", "cache_v_w128", "cache_v_w512",
        "cache_v_w2048", "w_in", "b_in", "w_s", "b_s", "ln_v_g", "ln_v_b", "w_o_a", "w_o_b", "w_out", "ln_g", "ln_b"]
_KEEPS = (128, 512, 512)


def kernel(**inputs):
    import concourse.bacc as bacc
    from concourse.bass_utils import run_bass_kernel_spmd

    nc = bacc.Bacc("TRN2", target_bir_lowering=False, num_devices=1)
    arrays = {}

    def given(name, a):
        arrays[name] = np.ascontiguousarray(a)
        return nc.dram_tensor(name, arrays[name].shape, F32, kind="ExternalInput").ap()

    shapes = {"y_prompt": (1, SEQ, D), "y_sample": (DEC_B, DEC_T, D)}
    for g, keep in enumerate(_KEEPS):
        for n in "kv":
            shapes[f"n{n}_p{g}"] = (1, 1, keep, HEADS, P)
            shapes[f"n{n}_s{g}"] = (1, DEC_B, DEC_T, HEADS, P)
    shapes["n_gv"] = (1, DEC_B, DEC_T, WIDTH)
    x = {n: given("in_" + n, inputs[n]) for n in _INS}
    c = [given("const_" + n, a) for n, a in zip(("cos", "sin", "mask", "smask", "tri", "tri8", "id"), tables())]
    o = {n: nc.dram_tensor("out_" + n, s, F32, kind="ExternalOutput").ap() for n, s in shapes.items()}
    build(nc, x["x_prompt"], x["x_sample"], [x[n] for n in _INS[2:5]], [x[n] for n in _INS[5:8]],
          *[x[n] for n in _INS[8:]], *c, o["y_prompt"], o["y_sample"],
          *[[o[f"n{n}_{w}{g}"] for g in range(3)] for n, w in (("k", "p"), ("v", "p"), ("k", "s"), ("v", "s"))],
          o["n_gv"])
    res = run_bass_kernel_spmd(nc, [arrays], core_ids=[0]).results[0]
    order = ["y_prompt", "y_sample"] + [f"n{n}_{w}{g}" for w in "ps" for g in range(3) for n in "kv"] + ["n_gv"]
    return tuple(res["out_" + n] for n in order)
```
